# Optimizing a Trainium2 kernel written in Bass

```python
import math
import jax, jax.numpy as jnp
from jax import lax
import numpy as np

D_MODEL = 2048
BATCH = 1
SEQ = 256
DEPTH = 2

HEAD_DIM = 128
GRID_W = 64
BLOCK = 128
EPS = 1e-6
A_HEADS = 8
NA_ROWS = 8
NA_COLS = 16
B_Q_HEADS = 8
B_KV_HEADS = 2
AXIAL_THETA = 10000.0
C_Q_HEADS = 12
C_KV_HEADS = 4
C_WINDOW = 128
C_SIDE_BLOCKS = -(-C_WINDOW // BLOCK)
D_DILATIONS = ((128, 1), (512, 4), (2048, 16))
D_GROUPS = len(D_DILATIONS)
D_SLOTS = 4
D_Q_HEADS = D_GROUPS * D_SLOTS
ROPE_THETA = 500000.0
ROPE_DIMS = HEAD_DIM // 4
FFN_HIDDEN = ((-(-8 * D_MODEL // 3)) + 255) // 256 * 256
N_EVEN = (DEPTH + 1) // 2
N_ODD = DEPTH // 2
AB_IN = (3 * A_HEADS + B_Q_HEADS + 2 * B_KV_HEADS) * HEAD_DIM
AB_OUT = (A_HEADS + B_Q_HEADS) * HEAD_DIM
CD_IN = (C_Q_HEADS + 2 * C_KV_HEADS + D_Q_HEADS + 2 * D_SLOTS) * HEAD_DIM
CD_OUT = (C_Q_HEADS + D_SLOTS) * HEAD_DIM

kernel_name = "hybrid_natten_axial_window_dilated_encoder"

def rms_norm(x, g):
    xf = x.astype(jnp.float32)
    y = xf * lax.rsqrt(jnp.mean(xf * xf, axis=-1, keepdims=True) + EPS)
    return (y * g.astype(jnp.float32)).astype(x.dtype)

def rope(x, pos, theta):
    r = x.shape[-1]
    half = r // 2
    inv = jnp.exp(-math.log(theta) * jnp.arange(half, dtype=jnp.float32) * (2.0 / r))
    ang = pos.astype(jnp.float32)[:, None] * inv[None, :]
    cos, sin = jnp.cos(ang), jnp.sin(ang)
    xf = x.astype(jnp.float32)
    x1, x2 = xf[..., :half], xf[..., half:]
    return jnp.concatenate([x1 * cos - x2 * sin, x1 * sin + x2 * cos], axis=-1).astype(x.dtype)

def partial_rope(x, pos):
    return jnp.concatenate([rope(x[..., :ROPE_DIMS], pos, ROPE_THETA), x[..., ROPE_DIMS:]], axis=-1)

def axial_rope(x, rows, cols):
    h = HEAD_DIM // 2
    return jnp.concatenate([rope(x[..., :h], rows, AXIAL_THETA), rope(x[..., h:], cols, AXIAL_THETA)], axis=-1)

def split_cols(h, widths):
    outs, start = [], 0
    for w in widths:
        outs.append(h[..., start:start + w])
        start += w
    return outs

def split_heads(h):
    b, s, c = h.shape
    return h.reshape(b, s, c // HEAD_DIM, HEAD_DIM).transpose(0, 2, 1, 3)

def merge_heads(o):
    b, n, s, dh = o.shape
    return o.transpose(0, 2, 1, 3).reshape(b, s, n * dh)

def neighbourhood_attention(q, k, v, rpb):
    b, h, s, dh = q.shape
    rows = s // GRID_W
    kr = min(NA_ROWS, rows)
    qg = q.reshape(b, h, rows, GRID_W, dh)
    kg = k.reshape(b, h, rows, GRID_W, dh)
    vg = v.reshape(b, h, rows, GRID_W, dh)
    cols = jnp.arange(GRID_W)
    col_start = jnp.clip(cols - NA_COLS // 2, 0, GRID_W - NA_COLS)
    col_idx = col_start[:, None] + jnp.arange(NA_COLS)[None, :]
    dc = col_idx - cols[:, None]
    scale = dh ** -0.5

    def row_block(r):
        r0 = jnp.clip(r - kr // 2, 0, rows - kr)
        kb = lax.dynamic_slice_in_dim(kg, r0, kr, axis=2)
        vb = lax.dynamic_slice_in_dim(vg, r0, kr, axis=2)
        kn = kb[:, :, :, col_idx]
        vn = vb[:, :, :, col_idx]
        qr = lax.dynamic_index_in_dim(qg, r, axis=2, keepdims=False)
        logits = jnp.einsum('bhwd,bhiwjd->bhwij', qr, kn,
                            preferred_element_type=jnp.float32) * scale
        dr = r0 + jnp.arange(kr) - r
        bias = rpb[:, dr[:, None, None] + NA_ROWS - 1, dc[None, :, :] + NA_COLS - 1]
        logits = logits + bias.transpose(0, 2, 1, 3)[None].astype(jnp.float32)
        p = jax.nn.softmax(logits.reshape(b, h, GRID_W, kr * NA_COLS), axis=-1)
        p = p.reshape(b, h, GRID_W, kr, NA_COLS).astype(v.dtype)
        return jnp.einsum('bhwij,bhiwjd->bhwd', p, vn)

    out = lax.map(row_block, jnp.arange(rows))
    return out.transpose(1, 2, 0, 3, 4).reshape(b, h, s, dh)

def dense_gqa(q, k, v):
    b, hq, s, dh = q.shape
    hkv = k.shape[1]
    g = hq // hkv
    nb = s // BLOCK
    scale = dh ** -0.5
    qb = q.reshape(b, hkv, g, nb, BLOCK, dh).transpose(3, 0, 1, 2, 4, 5)

    def blk(qi):
        logits = jnp.einsum('bkgqd,bksd->bkgqs', qi, k, preferred_element_type=jnp.float32) * scale
        p = jax.nn.softmax(logits, axis=-1).astype(v.dtype)
        return jnp.einsum('bkgqs,bksd->bkgqd', p, v)

    out = lax.map(blk, qb)
    return out.transpose(1, 2, 3, 0, 4, 5).reshape(b, hq, s, dh)

def window_gqa_sink(q, k, v, sink):
    b, hq, s, dh = q.shape
    hkv = k.shape[1]
    g = hq // hkv
    nb = s // BLOCK
    n_side = C_SIDE_BLOCKS
    n_band = 2 * n_side + 1
    scale = dh ** -0.5

    def band(t):
        tp = jnp.pad(t, ((0, 0), (0, 0), (n_side * BLOCK, n_side * BLOCK), (0, 0)))
        tb = tp.reshape(b, hkv, nb + 2 * n_side, BLOCK, dh)
        return jnp.concatenate([tb[:, :, j:j + nb] for j in range(n_band)], axis=3)

    kb, vb = band(k), band(v)
    qb = q.reshape(b, hkv, g, nb, BLOCK, dh)
    logits = jnp.einsum('bkgnqd,bknjd->bkgnqj', qb, kb,
                        preferred_element_type=jnp.float32) * scale
    blk = jnp.arange(nb)[:, None, None] * BLOCK
    qpos = blk + jnp.arange(BLOCK)[None, :, None]
    kpos = blk - n_side * BLOCK + jnp.arange(n_band * BLOCK)[None, None, :]
    valid = (jnp.abs(kpos - qpos) <= C_WINDOW) & (kpos >= 0) & (kpos < s)
    logits = jnp.where(valid, logits, -jnp.inf)
    sink_l = jnp.broadcast_to(sink.astype(jnp.float32).reshape(1, hkv, g, 1, 1, 1), logits.shape[:-1] + (1,))
    p = jax.nn.softmax(jnp.concatenate([logits, sink_l], axis=-1), axis=-1)[..., :-1]
    out = jnp.einsum('bkgnqj,bknjd->bkgnqd', p.astype(v.dtype), vb)
    return out.reshape(b, hq, s, dh)

def dilated_attention(q, k, v):
    b, _, s, dh = q.shape
    nb = s // BLOCK
    scale = dh ** -0.5
    offsets = []
    for w, d in D_DILATIONS:
        half = (w // 2) // d
        offsets.append(d * jnp.arange(-half, half + 1))
    qb = q.reshape(b, D_GROUPS, D_SLOTS, nb, BLOCK, dh).transpose(3, 0, 1, 2, 4, 5)

    def blk(args):
        i, qi = args
        t = i * BLOCK + jnp.arange(BLOCK)
        ms, dens, nums = [], [], []
        for gi, off in enumerate(offsets):
            idx = t[:, None] + off[None, :]
            valid = (idx >= 0) & (idx < s)
            idc = jnp.clip(idx, 0, s - 1)
            kg = k[:, :, idc]
            vg = v[:, :, idc]
            logits = jnp.einsum('bnqd,bnqjd->bnqj', qi[:, gi], kg,
                                preferred_element_type=jnp.float32) * scale
            logits = jnp.where(valid, logits, -jnp.inf)
            m = jnp.max(logits, axis=-1, keepdims=True)
            p = jnp.exp(logits - m)
            ms.append(m)
            dens.append(jnp.sum(p, axis=-1, keepdims=True))
            nums.append(jnp.einsum('bnqj,bnqjd->bnqd', p, vg.astype(jnp.float32)))
        m_all = jnp.max(jnp.stack(ms), axis=0)
        num = sum(jnp.exp(m - m_all) * n for m, n in zip(ms, nums))
        den = sum(jnp.exp(m - m_all) * dd for m, dd in zip(ms, dens))
        return (num / den).astype(v.dtype)

    out = lax.map(blk, (jnp.arange(nb), qb))
    return out.transpose(1, 2, 0, 3, 4).reshape(b, D_SLOTS, s, dh)

def mixer_ab(xn, w_in, w_out, a_qn, a_kn, a_rpb, b_qn, b_kn):
    s = xn.shape[1]
    h = xn @ w_in
    qa, ka, va, qb, kb, vb = [split_heads(t) for t in split_cols(
        h, [A_HEADS * HEAD_DIM] * 3 + [B_Q_HEADS * HEAD_DIM, B_KV_HEADS * HEAD_DIM, B_KV_HEADS * HEAD_DIM])]
    oa = neighbourhood_attention(rms_norm(qa, a_qn), rms_norm(ka, a_kn), va, a_rpb)
    pos = jnp.arange(s)
    rows, cols = pos // GRID_W, pos % GRID_W
    qb = axial_rope(rms_norm(qb, b_qn), rows, cols)
    kb = axial_rope(rms_norm(kb, b_kn), rows, cols)
    ob = dense_gqa(qb, kb, vb)
    return jnp.concatenate([merge_heads(oa), merge_heads(ob)], axis=-1) @ w_out

def mixer_cd(xn, w_in, w_out, c_qn, c_kn, c_sink, d_qn, d_kn):
    s = xn.shape[1]
    h = xn @ w_in
    qc, kc, vc, qd, kd, vd = [split_heads(t) for t in split_cols(
        h, [C_Q_HEADS * HEAD_DIM, C_KV_HEADS * HEAD_DIM, C_KV_HEADS * HEAD_DIM,
            D_Q_HEADS * HEAD_DIM, D_SLOTS * HEAD_DIM, D_SLOTS * HEAD_DIM])]
    pos = jnp.arange(s)
    oc = window_gqa_sink(partial_rope(rms_norm(qc, c_qn), pos), partial_rope(rms_norm(kc, c_kn), pos), vc, c_sink)
    od = dilated_attention(partial_rope(rms_norm(qd, d_qn), pos), partial_rope(rms_norm(kd, d_kn), pos), vd)
    return jnp.concatenate([merge_heads(oc), merge_heads(od)], axis=-1) @ w_out

def swiglu(xn, w_gate, w_up, w_down):
    return (jax.nn.silu(xn @ w_gate) * (xn @ w_up)) @ w_down

def setup_inputs(seed: int = 0) -> dict:
    key = jax.random.key(seed)
    ks = jax.random.split(key, 20)
    nrm = lambda k, shape, sc: jax.random.normal(k, shape, jnp.float32) * sc
    gain = lambda k, shape: 1.0 + 0.05 * jax.random.normal(k, shape, jnp.float32)
    return {
        "x": nrm(ks[0], (BATCH, SEQ, D_MODEL), 1.0),
        "attn_norm": gain(ks[1], (DEPTH, D_MODEL)),
        "ffn_norm": gain(ks[2], (DEPTH, D_MODEL)),
        "ab_w_in": nrm(ks[3], (N_EVEN, D_MODEL, AB_IN), D_MODEL ** -0.5),
        "ab_w_out": nrm(ks[4], (N_EVEN, AB_OUT, D_MODEL), AB_OUT ** -0.5),
        "a_q_norm": gain(ks[5], (N_EVEN, HEAD_DIM)),
        "a_k_norm": gain(ks[6], (N_EVEN, HEAD_DIM)),
        "a_rpb": nrm(ks[7], (N_EVEN, A_HEADS, 2 * NA_ROWS - 1, 2 * NA_COLS - 1), 0.5),
        "b_q_norm": gain(ks[8], (N_EVEN, HEAD_DIM)),
        "b_k_norm": gain(ks[9], (N_EVEN, HEAD_DIM)),
        "cd_w_in": nrm(ks[10], (N_ODD, D_MODEL, CD_IN), D_MODEL ** -0.5),
        "cd_w_out": nrm(ks[11], (N_ODD, CD_OUT, D_MODEL), CD_OUT ** -0.5),
        "c_q_norm": gain(ks[12], (N_ODD, HEAD_DIM)),
        "c_k_norm": gain(ks[13], (N_ODD, HEAD_DIM)),
        "c_sink": nrm(ks[14], (N_ODD, C_Q_HEADS), 0.5),
        "d_q_norm": gain(ks[15], (N_ODD, HEAD_DIM)),
        "d_k_norm": gain(ks[16], (N_ODD, HEAD_DIM)),
        "w_gate": nrm(ks[17], (DEPTH, D_MODEL, FFN_HIDDEN), D_MODEL ** -0.5),
        "w_up": nrm(ks[18], (DEPTH, D_MODEL, FFN_HIDDEN), D_MODEL ** -0.5),
        "w_down": nrm(ks[19], (DEPTH, FFN_HIDDEN, D_MODEL), FFN_HIDDEN ** -0.5),
    }

def reference(x, attn_norm, ffn_norm, ab_w_in, ab_w_out, a_q_norm, a_k_norm, a_rpb, b_q_norm, b_k_norm,
              cd_w_in, cd_w_out, c_q_norm, c_k_norm, c_sink, d_q_norm, d_k_norm, w_gate, w_up, w_down):
    for layer in range(DEPTH):
        j = layer // 2
        xn = rms_norm(x, attn_norm[layer])
        if layer % 2 == 0:
            x = x + mixer_ab(xn, ab_w_in[j], ab_w_out[j], a_q_norm[j], a_k_norm[j], a_rpb[j],
                             b_q_norm[j], b_k_norm[j])
        else:
            x = x + mixer_cd(xn, cd_w_in[j], cd_w_out[j], c_q_norm[j], c_k_norm[j], c_sink[j],
                             d_q_norm[j], d_k_norm[j])
        x = x + swiglu(rms_norm(x, ffn_norm[layer]), w_gate[layer], w_up[layer], w_down[layer])
    return x


_drawn_inputs = setup_inputs


def setup_inputs(seed=0):
    import zlib

    import numpy as np

    out = dict(_drawn_inputs(seed))
    spreads = {}
    factors = {'attn_norm': 2.739,
     'a_q_norm': 5.45,
     'a_k_norm': 6.192,
     'b_q_norm': 8.0,
     'b_k_norm': 8.0,
     'c_q_norm': 8.0,
     'c_k_norm': 8.0,
     'c_sink': 8.0,
     'd_q_norm': 8.0,
     'd_k_norm': 8.0}
    for name, (base, spread) in spreads.items():
        noise = np.random.default_rng([zlib.crc32(name.encode()), seed]).standard_normal(out[name].shape)
        drawn = base * np.exp(spread * noise) if base else spread * noise
        out[name] = __import__('jax').numpy.asarray(drawn.astype(out[name].dtype))
    for name, factor in factors.items():
        out[name] = (out[name] * factor).astype(out[name].dtype)
    return out
```

```python
from contextlib import ExitStack

import concourse.bass as bass
from concourse import mybir

F32 = mybir.dt.float32
F32R = mybir.dt.float32r
BF16 = mybir.dt.bfloat16
ALU = mybir.AluOpType
ACT = mybir.ActivationFunctionType
AX = mybir.AxisListType

P = 128
SEQ = 256
TOK = SEQ // P
D_MODEL = 2048
FFN = 5632
DH = 128
N = 512
KC = D_MODEL // P
HC = FFN // P
XT = D_MODEL // N
HT = FFN // N
EPS = 1e-6
SCALE = DH ** -0.5

RING = 4
LEAD = RING - 1
UC = 2
KU = KC // UC
DOWN_UNITS = [(k, 2) for k in range(0, 20, 2)] + [(k, 1) for k in range(20, 24)] + [(k, 2) for k in range(24, HC, 2)]
DU = len(DOWN_UNITS)
assert DU % RING == 0 and KU % RING == 0 and sum(n for _, n in DOWN_UNITS) == HC

AB_TILES = [(8, "kv_b", 0), (6, "q_b", 0), (7, "q_b", 4), (0, "q_a", 0), (2, "k_a", 0), (4, "v_a", 0),
            (1, "q_a", 4), (3, "k_a", 4), (5, "v_a", 4)]
CD_TILES = [(8, "k_d", 0), (5, "q_d", 0), (6, "q_d", 4), (7, "q_d", 8), (3, "k_c", 0), (4, "v_c", 0),
            (0, "q_c", 0), (1, "q_c", 4), (2, "q_c", 8), (9, "v_d", 0)]
AB_ITEMS = ([("b", h, 22 + 2 * h, 27 + 2 * h, 29 + 2 * h) for h in range(8)]
            + [("a", h, t, t + 4, t + 6) for h, t in enumerate((45, 47, 49, 51, 68, 69, 70, 71))])
CD_ITEMS = ([("d", s, 37 + 4 * s, 42 + 4 * s, 80 + s) for s in range(4)]
            + [("c", h, *ticks) for h, ticks in enumerate(
                [(61, 65, 67), (63, 67, 69), (65, 69, 71), (67, 71, 73), (69, 73, 75), (71, 76, 77), (73, 77, 78),
                 (74, 78, 79), (76, 80, 82), (77, 81, 83), (78, 82, 84), (79, 83, 85)])])
AB_CHUNKS = list(range(8, 16)) + list(range(8))
CD_CHUNKS = list(range(8)) + list(range(12, 16)) + list(range(8, 12))
CHUNK_OF = {"a": 0, "b": 8, "c": 0, "d": 12}
MASK_OF = {"c": 0, "d": 1}


class Mixer:

    def __init__(self, tiles, items, chunks, fills, heads_before, qk_before, last_users):
        self.tiles, self.items, self.chunks = tiles, items, chunks
        self.ticks = KU * (len(tiles) + 1)
        self.head0 = heads_before
        self.qk0 = qk_before
        self.qk_tiles = [p for p, (_, kind, _) in enumerate(tiles) if kind[0] in "qk"]
        self.v_tiles = [p for p, (_, kind, _) in enumerate(tiles) if "v" in kind]
        self.fill = {}
        for t in range(self.ticks + 8):
            for p in self.qk_tiles:
                if t == self.turn_tick(p):
                    for half in range(2):
                        self.fill["qk", p, half] = fills
                        fills += 1
            for n, (_, _, _, at, _) in enumerate(items):
                if t == at:
                    self.fill["p", n] = fills
                    fills += 1
        self.fills = fills
        assert not {at for *_, at, _ in items} & {self.turn_tick(p) for p in self.qk_tiles}
        self.pv = sorted(range(len(items)), key=lambda n: (items[n][4], n))
        self.pv_rank = {n: r for r, n in enumerate(self.pv)}
        self.banks, self.bank_waits = [], []
        last = dict(last_users)
        for n, (kind, h, *_) in enumerate(items):
            self.banks.append([0, 1, 2] if kind == "d" else [n % 3])
            waits = {}
            for b in self.banks[n]:
                if b in last:
                    what, count = last[b]
                    waits[what] = max(waits.get(what, 0), count)
                last[b] = ("biased", h + 1) if kind == "a" else ("exp_done", heads_before + n + 1)
            self.bank_waits.append(waits)
        self.last_users = last

    def exp_tick(self, n):
        kind, _, at, *_ = self.items[n]
        return at + (3 if kind == "d" else 2)

    def qk_tick(self, p, after):
        return KU * (p + 1) + after

    def turn_tick(self, p):
        return self.qk_tick(p, 3 if self.tiles[p][1:] in (("k_a", 4), ("q_c", 8)) else 4)

    def tile_of(self, kind, head):
        for p, (_, k, h0) in enumerate(self.tiles):
            if k == kind and h0 <= head < h0 + 4:
                return p
        raise KeyError((kind, head))


def plan():
    ph, u, a, b, f, th = {}, 0, 0, 0, 2 * XT, 2 * XT
    mixers = []
    heads = qk = 0
    last_users = {}
    for layer, (tiles, items, chunks) in enumerate(((AB_TILES, AB_ITEMS, AB_CHUNKS), (CD_TILES, CD_ITEMS, CD_CHUNKS))):
        m = Mixer(tiles, items, chunks, f, heads, qk, last_users)
        mixers.append(m)
        ph["in", layer] = dict(u=u, a=a, b=b, f=f, th=th)
        u, a, f = u + KU * len(tiles), a + len(tiles), m.fills
        heads, qk, last_users = heads + len(items), qk + len(m.qk_tiles), m.last_users
        ph["out", layer] = dict(u=u, a=a, b=b, f=f, th=th)
        u, a, f, th = u + KU * XT, a + XT, f + 2 * XT, th + 2 * XT
        ph["up", layer] = dict(u=u, a=a, b=b, f=f, th=th)
        u, a, b, f, th = u + 2 * KU * HT, a + HT, b + HT, f + 2 * HT, th + 2 * HT
        ph["down", layer] = dict(u=u, a=a, b=b, f=f, th=th)
        u, a = u + DU * XT, a + XT
        if layer == 0:
            f, th = f + 2 * XT, th + 2 * XT
    return ph, mixers, u


class Steps:

    def __init__(self, eng, sem):
        self.eng, self.sem, self.n = eng, sem, 0

    def then(self, ins):
        self.n += 1
        ins.then_inc(self.sem, 1)
        self.eng.wait_ge(self.sem, self.n)


def encoder(nc, x, attn_gain, ffn_gain, ab_w_in, ab_w_out, a_gain, a_bias, b_gain, cd_w_in, cd_w_out,
            cd_gain, cd_gain_rot, sink, w_gate, w_up, w_down, ident, ident16, masks, axial, partial, out):
    ph, mixers, n_units = plan()

    with ExitStack() as ctx:
        def sb(name, shape, dt=F32, c=ctx):
            return c.enter_context(nc.sbuf_tensor(name, shape, dt))

        def sem(name):
            return ctx.enter_context(nc.semaphore(name))

        psum = ctx.enter_context(nc.psum_tensor("psum", [P, 8, N], F32))
        ACC = [psum[:, 0:2, :], psum[:, 2:4, :]]
        SCORES = 2
        TBANK = 5
        OBANK = 7

        x_res = sb("x_res", [P, TOK, D_MODEL])
        xt_hi = sb("xt_hi", [P, KC, SEQ], F32R)
        xt_lo = sb("xt_lo", [P, KC, SEQ], F32R)
        w_raw = sb("w_raw", [P, RING, UC, N])
        w_hi = sb("w_hi", [P, RING, UC, N], F32R)
        w_lo = sb("w_lo", [P, RING, UC, N], F32R)
        stage = [sb(f"stage{k}", [P, TOK, N]) for k in range(3)]
        probs = sb("probs", [P, 3, TOK, SEQ])
        mask_sb = sb("mask_sb", [P, 4, TOK, SEQ], BF16)
        ident_sb = sb("ident_sb", [P, P])
        ident16_sb = sb("ident16_sb", [P, P], BF16)
        gain_x = sb("gain_x", [P, 4, KC])
        gain_a = sb("gain_a", [P, 2])
        sink_sb = sb("sink_sb", [P, 12])
        neg_sink = sb("neg_sink", [P, 12])
        ssq = sb("ssq", [P, TOK, XT])
        msq = sb("msq", [P, TOK])
        msq_eps = sb("msq_eps", [P, TOK])
        rstd = sb("rstd", [P, 4, TOK])
        head_ssq = sb("head_ssq", [P, TOK, 4])
        head_eps = sb("head_eps", [P, TOK, 4])
        head_rstd = sb("head_rstd", [P, TOK, 4])
        table_warm = sb("table_warm", [P, 1])
        minus_half = sb("minus_half", [P, TOK * 4])
        rowmax = sb("rowmax", [P, 4, TOK])
        negmax = sb("negmax", [P, 4, TOK])
        denom = sb("denom", [P, 4, TOK])
        sinkexp = sb("sinkexp", [P, 4, TOK])
        rdenom = sb("rdenom", [P, 4, TOK])

        with ExitStack() as ab:
            sb("ab_pad0", [P, KC, SEQ], c=ab)
            qt_b = sb("qt_b", [P, 8, SEQ], c=ab)
            kt_b = sb("kt_b", [P, 2, SEQ], c=ab)
            v_b = sb("v_b", [P, TOK, 2 * DH], c=ab)
            qt_a = sb("qt_a", [P, 8, SEQ], c=ab)
            kt_a = sb("kt_a", [P, 8, SEQ], c=ab)
            sb("ab_pad1", [P, KC, SEQ], c=ab)
            v_a = sb("v_a", [P, TOK, 8 * DH], c=ab)
            bias_sb = sb("bias_sb", [P, 2, TOK, SEQ], c=ab)
            logit_sb = sb("logit_sb", [P, 2, TOK, SEQ], c=ab)
            ab_pt = sb("ab_pt", [P, 2, TOK, SEQ], c=ab)
            axial_sb = sb("axial_sb", [P, 4, TOK, DH], c=ab)
            b_gain_sb = sb("b_gain_sb", [P, 4, DH], c=ab)
        with ExitStack() as cd:
            sb("cd_pad0", [P, KC, SEQ], c=cd)
            kt_c = sb("kt_c", [P, 4, SEQ], c=cd)
            v_c = sb("v_c", [P, TOK, 4 * DH], c=cd)
            qt_c = sb("qt_c", [P, 12, SEQ], c=cd)
            kt_d = sb("kt_d", [P, 4, SEQ], c=cd)
            v_d = sb("v_d", [P, TOK, 4 * DH], c=cd)
            sb("cd_pad1", [P, KC, SEQ], c=cd)
            qt_d = sb("qt_d", [P, 12, SEQ], c=cd)
            d_pt = sb("d_pt", [P, 4, TOK, SEQ], c=cd)
            cd_pt = sb("cd_pt", [P, 2, TOK, SEQ], c=cd)
            partial_sb = sb("partial_sb", [P, 4, 2, TOK, 32], c=cd)
            cd_gain_sb = sb("cd_gain_sb", [P, 4, DH], c=cd)
        ht_hi = sb("ht_hi", [P, HC, SEQ], F32R)
        ht_lo = sb("ht_lo", [P, HC, SEQ], F32R)
        cd_rot_sb = sb("cd_rot_sb", [P, 4, 2, 32])

        x_loaded = [sem(f"x_loaded{j}") for j in range(XT)]
        ident_loaded = sem("ident_loaded")
        const_loaded = sem("const_loaded")
        const2_loaded = sem("const2_loaded")
        cd_const_loaded = sem("cd_const_loaded")
        bias_loaded = [sem(f"bias_loaded{k}") for k in range(2)]
        w_loaded = [sem(f"w_loaded{s}") for s in range(RING)]
        hi_ready = sem("hi_ready")
        lo_ready = sem("lo_ready")
        unit_used = sem("unit_used")
        acc_done = [sem("acc0_done"), sem("acc1_done")]
        acc_free = [sem("acc0_free"), sem("acc1_free")]
        t_full = sem("t_full")
        t_hi = sem("t_hi")
        t_read = [sem("t0_read"), sem("t1_read")]
        x_stored = sem("x_stored")
        ssq_done = sem("ssq_done")
        msq_ready = sem("msq_ready")
        rstd_ready = sem("rstd_ready")
        sq_ready = sem("sq_ready")
        hssq_ready = sem("hssq_ready")
        hrstd_ready = sem("hrstd_ready")
        qk_normed = sem("qk_normed")
        l_full = sem("l_full")
        biased = sem("biased")
        negmax_ready = sem("negmax_ready")
        exp_done = sem("exp_done")
        probs_ready = sem("probs_ready")
        o_full = sem("o_full")
        ot_hi_ready = sem("ot_hi_ready")
        ot_ready = sem("ot_ready")
        dve_step = sem("dve_step")
        pool_step = sem("pool_step")
        stored = sem("stored")

        def t_bank(f):
            return psum[:, TBANK + f % 2, :].rearrange("p (c t) -> p c t", c=2)

        def wait_read(eng, *fills):
            for f in fills:
                eng.wait_ge(t_read[f % 2], f // 2 + 1)

        SECOND_O = {("c", 8), ("c", 9)}
        SECOND_O_SCORES = 1

        def o_bank(kind, h):
            bank = SCORES + SECOND_O_SCORES if (kind, h) in SECOND_O else OBANK
            return psum[:, bank, 0:SEQ]

        def heads_of(s, n):
            return s[:, :, 0:n * DH].rearrange("p t (h d) -> p t h d", d=DH)

        def qk_dest(kind, h0, half):
            if kind == "kv_b":
                return kt_b[:, half:half + 1, :]
            dst = {"q_b": qt_b, "q_a": qt_a, "k_a": kt_a, "q_c": qt_c, "k_c": kt_c, "q_d": qt_d, "k_d": kt_d}[kind]
            return dst[:, h0 + 2 * half:h0 + 2 * half + 2, :]

        def pt_of(layer, n):
            if layer == 0:
                return ab_pt[:, n % 2]
            return d_pt[:, n] if n < 4 else cd_pt[:, n % 2]

        def residual_acc(layer, name, n):
            p, units = ph[name, layer], KU if name == "out" else DU
            return p["a"] + n + 1, p["u"] + (n + 1) * units

        RES = {("out", 0): 0, ("down", 0): XT, ("out", 1): 2 * XT, ("down", 1): 3 * XT}
        LN_OF = {("out", 0): 1, ("down", 0): 2, ("out", 1): 3}
        GAIN_OF = [0, 2, 1, 3]

        w_in = [ab_w_in, cd_w_in]
        w_out = [ab_w_out, cd_w_out]
        CONST, CONST2 = 16, 16 * 8
        block = ctx.enter_context(nc.Block())

        @block.sync
        def _(sp):
            def load(u, slot, src, c0, n, cols, first=False):
                if not first:
                    sp.wait_ge(lo_ready, u - RING + 1)
                rows = src[c0 * P:(c0 + n) * P, cols].rearrange("(c p) n -> p c n", p=P)
                sp.dma_start(w_raw[:, slot, 0:n, :], rows).then_inc(w_loaded[slot], 16)

            def load_input(j):
                xv = x.rearrange("(t p) n -> p t n", p=P)
                sp.dma_start(x_res[:, :, j * N:(j + 1) * N], xv[:, :, j * N:(j + 1) * N]).then_inc(x_loaded[j], 16)

            constants = [(axial_sb[:], axial, const2_loaded), (b_gain_sb[:], b_gain, const2_loaded),
                         (gain_a[:], a_gain, const2_loaded), (sink_sb[:], sink, const2_loaded),
                         (mask_sb[:], masks, const2_loaded), (ident16_sb[:], ident16, const2_loaded),
                         (gain_x[:, 2:4, :], ffn_gain, const2_loaded), (cd_rot_sb[:], cd_gain_rot, const2_loaded),
                         (bias_sb[:, 0], a_bias[0], bias_loaded[0]), (bias_sb[:, 1], a_bias[1], bias_loaded[1])]

            sp.dma_start(ident_sb[:], ident).then_inc(ident_loaded, 16)
            load_input(0)
            for layer in range(2):
                for p, (col, _, _) in enumerate(mixers[layer].tiles):
                    for k in range(KU):
                        u = ph["in", layer]["u"] + KU * p + k
                        if 1 <= u < XT:
                            load_input(u)
                        load(u, k % RING, w_in[layer], UC * k, UC, slice(col * N, col * N + N), first=u < RING)
                        if RING <= u < RING + len(constants) // 2:
                            for dst, src, loaded in constants[2 * (u - RING):2 * (u - RING) + 2]:
                                sp.dma_start(dst, src).then_inc(loaded, 16)
                with sp.Fori(1, XT + 1) as n1:
                    for k in range(KU):
                        load(n1 * KU + (ph["out", layer]["u"] + k - KU), k % RING, w_out[layer],
                             mixers[layer].chunks[UC * k], UC, bass.ds(n1 * N - N, N))
                with sp.Fori(0, HT) as i:
                    for half, w in enumerate((w_gate[layer], w_up[layer])):
                        for k in range(KU):
                            load(i * (2 * KU) + (ph["up", layer]["u"] + half * KU + k), k % RING, w, UC * k, UC,
                                 bass.ds(i * N, N))
                with sp.Fori(0, XT) as n:
                    for k, (c0, nc_) in enumerate(DOWN_UNITS):
                        load(n * DU + (ph["down", layer]["u"] + k), k % RING, w_down[layer], c0, nc_, bass.ds(n * N, N))

        @block.tensor
        def _(pe):
            def unit(u, slot, hi, lo, chunks, pair, use, first, last):
                pe.wait_ge(lo_ready, u + 1)
                for tok in range(TOK):
                    if first:
                        pe.wait_ge(acc_free[pair], use * TOK + (tok + 1 - TOK)) if use_positive(use, tok) else None
                    ts = slice(tok * P, tok * P + P)
                    for c, chunk in enumerate(chunks):
                        acc = ACC[pair][:, tok, :]
                        nc.tensor.matmul(acc, hi[:, chunk, ts], w_hi[:, slot, c, :], start=first and c == 0, stop=False)
                        nc.tensor.matmul(acc, hi[:, chunk, ts], w_lo[:, slot, c, :], start=False, stop=False)
                        end = last and c == len(chunks) - 1
                        mm = nc.tensor.matmul(acc, lo[:, chunk, ts], w_hi[:, slot, c, :], start=False, stop=end)
                    if last and tok == 0:
                        mm.then_inc(acc_done[pair], 1)
                mm.then_inc(unit_used, 1)

            def use_positive(use, tok):
                return not isinstance(use, int) or use > 0

            def wait_t_free(f):
                if f >= 2:
                    wait_read(pe, f - 2)

            def transposes(src, bank):
                for c in range(2):
                    for tok in range(TOK):
                        mm = nc.tensor.transpose(t_bank(bank)[:, c, tok * P:tok * P + P], src(c, tok), ident_sb[:])
                mm.then_inc(t_full, 1)

            def residual_transposes(layer, name, n):
                pe.wait_ge(acc_free[0], n * 2 + (2 * ph[name, layer]["a"] + 2))
                for half in range(2):
                    pe.wait_ge(t_read[half], n + ph[name, layer]["f"] // 2)
                    transposes(lambda c, tok: stage[0][:, tok, (2 * half + c) * P:(2 * half + c + 1) * P], half)

            def hidden_transposes(layer, i):
                pe.wait_ge(acc_free[1], i * 2 + (2 * ph["up", layer]["b"] + 2))
                for half in range(2):
                    pe.wait_ge(t_read[half], i + ph["up", layer]["f"] // 2)
                    transposes(lambda c, tok: stage[1][:, tok, (2 * half + c) * P:(2 * half + c + 1) * P], half)

            def attention(layer, t):
                m = mixers[layer]
                for q, p in enumerate(m.qk_tiles):
                    if t == m.turn_tick(p):
                        _, kind, h0 = m.tiles[p]
                        pe.wait_ge(qk_normed, m.qk0 + q + 1)
                        src = stage[2] if kind in ("q_a", "k_a") else stage[0]
                        for half in range(2):
                            f = m.fill["qk", p, half]
                            wait_t_free(f)
                            if kind == "kv_b":
                                for tok in range(TOK):
                                    mm = nc.tensor.transpose(t_bank(f)[:, 0, tok * P:tok * P + P],
                                                             src[:, tok, half * P:half * P + P], ident_sb[:])
                                mm.then_inc(t_full, 1)
                            else:
                                transposes(lambda c, tok: src[:, tok, (2 * half + c) * P:(2 * half + c + 1) * P], f)
                for n, (kind, h, _, at, _) in enumerate(m.items):
                    if t == at:
                        f = m.fill["p", n]
                        pe.wait_ge(probs_ready, m.head0 + n + 1)
                        wait_t_free(f)
                        slot = 0 if kind == "d" else n % 3
                        transposes(lambda kt, qt: probs[:, slot, qt, kt * P:kt * P + P], f)
                for n in m.pv:
                    kind, h, _, _, at = m.items[n]
                    if t == at:
                        r = m.pv_rank[n]
                        wait_read(pe, m.fill["p", n])
                        vt = {"a": v_a, "b": v_b, "c": v_c, "d": v_d}[kind]
                        vh = {"a": h, "b": h // 4, "c": h // 3, "d": h}[kind]
                        vp = {"a": m.tile_of("v_a", h) if kind == "a" else 0, "b": 0,
                              "c": m.v_tiles[0], "d": m.v_tiles[-1]}[kind]
                        pe.wait_ge(acc_free[0], TOK * (ph["in", layer]["a"] + vp + 1))
                        if (kind, h) in SECOND_O:
                            last = max(n for n, banks in enumerate(m.banks) if SECOND_O_SCORES in banks)
                            pe.wait_ge(exp_done, m.head0 + last + 1)
                            before = [m.pv_rank[i] for i, item in enumerate(m.items)
                                      if item[:2] in SECOND_O and m.pv_rank[i] < r]
                            if before:
                                pe.wait_ge(ot_ready, m.head0 + max(before) + 1)
                        elif m.head0 + r:
                            pe.wait_ge(ot_ready, m.head0 + r)
                        for kt in range(TOK):
                            mm = nc.tensor.matmul(o_bank(kind, h), vt[:, kt, vh * DH:vh * DH + DH],
                                                  pt_of(layer, n)[:, kt, :], start=kt == 0, stop=kt == TOK - 1)
                        mm.then_inc(o_full, 1)
                for n, (kind, h, at, *_) in enumerate(m.items):
                    if t == at:
                        need = {"a": ("k_a", h), "b": ("q_b", h), "c": ("q_c", h), "d": ("q_d", 8 + h)}[kind]
                        p = m.tile_of(*need)
                        wait_read(pe, m.fill["qk", p, 0], m.fill["qk", p, 1])
                        if kind in "cd" and n in (0, 4):
                            pe.wait_ge(const2_loaded, CONST2)
                        for what, count in m.bank_waits[n].items():
                            pe.wait_ge({"biased": biased, "exp_done": exp_done}[what], count)
                        for g, b in enumerate(m.banks[n]):
                            qt = {"a": qt_a, "b": qt_b, "c": qt_c, "d": qt_d}[kind]
                            kt = {"a": kt_a, "b": kt_b, "c": kt_c, "d": kt_d}[kind]
                            qh = 4 * g + h
                            kh = {"a": h, "b": h // 4, "c": h // 3, "d": h}[kind]
                            for tok in range(TOK):
                                dst = psum[:, SCORES + b, tok * SEQ:tok * SEQ + SEQ]
                                if kind in "cd":
                                    nc.tensor.matmul(dst, ident16_sb[:], mask_sb[:, MASK_OF[kind] + g, tok, :],
                                                     start=True, stop=False)
                                mm = nc.tensor.matmul(dst, qt[:, qh, tok * P:tok * P + P], kt[:, kh, :],
                                                      start=kind in "ab", stop=True)
                        mm.then_inc(l_full, 1)

            def input_transposes(j):
                pe.wait_ge(x_loaded[j], 16)
                for half in range(2):
                    wait_t_free(2 * j + half)
                    transposes(lambda c, tok: x_res[:, tok, (4 * j + 2 * half + c) * P:(4 * j + 2 * half + c + 1) * P],
                               half)

            pe.wait_ge(ident_loaded, 16)
            input_transposes(0)
            for layer in range(2):
                m, pi, po, pu, pd = mixers[layer], *(ph[s, layer] for s in ("in", "out", "up", "down"))
                for p in range(len(m.tiles)):
                    for k in range(KU):
                        t = KU * p + k
                        if layer == 0 and p == 0 and k % 2 == 0 and k // 2 + 1 < XT:
                            input_transposes(k // 2 + 1)
                        if p == 0:
                            wait_read(pe, (pi["f"] if layer == 0 else ph["down", 0]["f"] + 2 * XT) - 2 * XT + k)
                        unit(pi["u"] + t, k % RING, xt_hi, xt_lo, (2 * k, 2 * k + 1), 0, pi["a"] + p, k == 0, k == KU - 1)
                        attention(layer, t)
                        if layer == 1 and t == 1:
                            residual_transposes(0, "down", XT - 1)

                def out_tile(n, first):
                    for k in range(KU):
                        if first:
                            ready = max(m.pv_rank[i] for i, (kind, h, *_) in enumerate(m.items)
                                        if CHUNK_OF[kind] + h in m.chunks[2 * k:2 * k + 2])
                            pe.wait_ge(ot_ready, m.head0 + ready + 1)
                        unit(n * KU + (po["u"] + k), k % RING, ht_hi, ht_lo, m.chunks[2 * k:2 * k + 2], 0,
                             n + po["a"], k == 0, k == KU - 1)
                        if first:
                            attention(layer, KU * len(m.tiles) + k)
                        elif k == 1:
                            residual_transposes(layer, "out", n - 1)

                out_tile(0, True)
                with pe.Fori(0, XT - 1) as j:
                    out_tile(j + 1, False)

                def up_tile(i, first):
                    for half in range(2):
                        for k in range(KU):
                            if first and half == 0:
                                wait_read(pe, po["f"] + k)
                            unit(i * (2 * KU) + (pu["u"] + half * KU + k), k % RING, xt_hi, xt_lo, (2 * k, 2 * k + 1),
                                 half, i + (pu["a"] if half == 0 else pu["b"]), k == 0, k == KU - 1)
                            if half == 0 and k == 1:
                                residual_transposes(layer, "out", XT - 1) if first else hidden_transposes(layer, i - 1)

                up_tile(0, True)
                with pe.Fori(0, HT - 1) as j:
                    up_tile(j + 1, False)

                def down_tile(n, first):
                    for k, (c0, nch) in enumerate(DOWN_UNITS):
                        if first:
                            wait_read(pe, pu["f"] + (c0 + nch - 1) // 2)
                        unit(n * DU + (pd["u"] + k), k % RING, ht_hi, ht_lo, range(c0, c0 + nch), 0, n + pd["a"],
                             k == 0, k == DU - 1)
                        if k == 1:
                            if first:
                                hidden_transposes(layer, HT - 1)
                            elif layer == 0:
                                residual_transposes(layer, "down", n - 1)

                down_tile(0, True)
                with pe.Fori(0, XT - 1) as j:
                    down_tile(j + 1, False)

        @block.scalar
        def _(act):
            def split(u, slot, n=UC, ring_full=True):
                act.wait_ge(w_loaded[slot], loads(u, slot))
                if ring_full:
                    act.wait_ge(unit_used, u - RING + 1)
                nc.scalar.activation(w_hi[:, slot, 0:n, :], w_raw[:, slot, 0:n, :], ACT.Copy).then_inc(hi_ready, 1)

            def loads(u, slot):
                if isinstance(u, int):
                    return 16 * (u // RING + 1)
                return u * (16 // RING) + 16 - (16 // RING) * slot

            def tok_done(pair, tok, uses, units):
                if tok == 0:
                    act.wait_ge(acc_done[pair], uses)
                else:
                    act.wait_ge(unit_used, units)

            def fill_to_xt(f_count, bank, chunk, gain, gain_col):
                act.wait_ge(t_full, f_count)
                for c in range(2):
                    ins = nc.scalar.activation(chunk_of(xt_hi, chunk, c), t_bank(bank)[:, c, :], ACT.Copy,
                                               scale=gain_of(gain, gain_col, c))
                ins.then_inc(t_hi, 1)

            def chunk_of(t, chunk, c):
                return t[:, bass.ds(chunk + c, 1), :].rearrange("p c t -> p (c t)")

            def gain_of(gain, col, c):
                return gain_x[:, gain, bass.ds(col + c, 1)]

            def residual_ssq(layer, name, n):
                act.wait_ge(acc_free[0], n * 2 + (2 * ph[name, layer]["a"] + 2))
                act.wait_ge(ssq_done, n + XT * LN_OF[name, layer])
                for tok in range(TOK):
                    ins = nc.scalar.activation(stage[2][:, tok, :], stage[0][:, tok, :], ACT.Square,
                                               accum_out=ssq[:, tok, bass.ds(n, 1)])
                ins.then_inc(ssq_done, 1)

            def residual_hi(layer, name, n):
                gain = GAIN_OF[LN_OF[name, layer]]
                for half in range(2):
                    fill_to_xt(n * 2 + (ph[name, layer]["f"] + half + 1), half, n * 4 + 2 * half, gain, n * 4 + 2 * half)

            def store(n):
                dst = out.rearrange("(t p) n -> p t n", p=P)
                for tok in range(TOK):
                    act.wait_ge(acc_free[0], n * 2 + (2 * ph["down", 1]["a"] + tok + 1))
                    act.dma_start(dst[:, tok, bass.ds(n * N, N)], stage[0][:, tok, :]).then_inc(stored, 16)

            def silu(layer, i):
                pu = ph["up", layer]
                for tok in range(TOK):
                    tok_done(0, tok, i + (pu["a"] + 1), i * (2 * KU) + (pu["u"] + KU))
                    ins = nc.scalar.activation(stage[0][:, tok, :], ACC[0][:, tok, :], ACT.Silu,
                                               scale=rstd[:, 2 * layer + 1, tok:tok + 1])
                    ins.then_inc(acc_free[0], 1)

            def hidden_hi(layer, i):
                for half in range(2):
                    act.wait_ge(t_full, i * 2 + (ph["up", layer]["f"] + half + 1))
                    nc.scalar.activation(ht_hi[:, bass.ds(i * 4 + 2 * half, 2), :], t_bank(half),
                                         ACT.Copy).then_inc(t_hi, 1)

            def evacuate(layer, p):
                m, pi = mixers[layer], ph["in", layer]
                _, kind, h0 = m.tiles[p]
                if p == 0:
                    act.wait_ge(rstd_ready, 2 * layer + 1)
                    act.wait_ge(x_stored, RES["out", layer] + 1)
                for tok in range(TOK):
                    tok_done(0, tok, pi["a"] + p + 1, pi["u"] + KU * (p + 1))
                    scale = rstd[:, 2 * layer, tok:tok + 1]
                    acc = ACC[0][:, tok, :]
                    if kind == "kv_b":
                        nc.scalar.activation(v_b[:, tok, :], acc[:, 2 * DH:], ACT.Copy, scale=scale)
                        nc.scalar.activation(stage[0][:, tok, 0:2 * DH], acc[:, 0:2 * DH], ACT.Copy,
                                             scale=scale).then_inc(acc_free[0], 1)
                    elif kind[0] == "v":
                        dst = {"v_a": v_a, "v_c": v_c, "v_d": v_d}[kind][:, tok, h0 * DH:h0 * DH + N]
                        nc.scalar.activation(dst, acc, ACT.Copy, scale=scale).then_inc(acc_free[0], 1)
                    else:
                        nc.scalar.activation(stage[0][:, tok, :], acc, ACT.Copy, scale=scale).then_inc(acc_free[0], 1)

            def attention(layer, t):
                m = mixers[layer]
                for n in m.pv:
                    kind, h, _, _, at = m.items[n]
                    if t == at + 1:
                        r = m.pv_rank[n]
                        act.wait_ge(o_full, m.head0 + r + 1)
                        nc.scalar.activation(ht_hi[:, CHUNK_OF[kind] + h, :], o_bank(kind, h),
                                             ACT.Copy).then_inc(ot_hi_ready, 1)
                for q, p in enumerate(m.qk_tiles):
                    _, kind, h0 = m.tiles[p]
                    cols = 2 * DH if kind == "kv_b" else N
                    if t == m.qk_tick(p, 0):
                        act.wait_ge(acc_free[0], 2 * (ph["in", layer]["a"] + p + 1))
                        nc.scalar.activation(stage[1][:, :, 0:cols], stage[0][:, :, 0:cols],
                                             ACT.Square).then_inc(sq_ready, 1)
                    if t == m.turn_tick(p) + 1:
                        for half in range(2):
                            f = m.fill["qk", p, half]
                            act.wait_ge(t_full, f + 1)
                            src = t_bank(f)[:, 0:1, :] if kind == "kv_b" else t_bank(f)
                            if kind in ("q_a", "k_a"):
                                g = gain_a[:, 0:1] if kind == "q_a" else gain_a[:, 1:2]
                                if q == 3 and half == 0:
                                    act.wait_ge(const2_loaded, CONST2)
                                ins = nc.scalar.activation(qk_dest(kind, h0, half), src, ACT.Copy, scale=g)
                            else:
                                ins = nc.scalar.activation(qk_dest(kind, h0, half), src, ACT.Copy)
                            ins.then_inc(t_read[f % 2], 1)
                for n, (kind, h, _, at, _) in enumerate(m.items):
                    if t == at + 1:
                        f = m.fill["p", n]
                        act.wait_ge(t_full, f + 1)
                        if kind != "d" and n >= (2 if layer == 0 else 6):
                            act.wait_ge(o_full, m.head0 + m.pv_rank[n - 2] + 1)
                        nc.scalar.activation(pt_of(layer, n), t_bank(f), ACT.Copy).then_inc(t_read[f % 2], 1)
                for n, (kind, h, at, *_) in enumerate(m.items):
                    if t == m.exp_tick(n):
                        act.wait_ge(negmax_ready, m.head0 + n + 1)
                        banks = m.banks[n]
                        s = n % 4
                        for tok in range(TOK):
                            bias, den = negmax[:, s, tok:tok + 1], denom[:, s, tok:tok + 1]
                            if kind == "d":
                                src = psum[:, SCORES:SCORES + 3, tok * SEQ:tok * SEQ + SEQ]
                                ins = nc.scalar.activation(probs[:, :, tok, :], src, ACT.Exp, bias=bias, scale=SCALE,
                                                           accum_out=den)
                            elif kind == "a":
                                ins = nc.scalar.activation(probs[:, n % 3, tok, :], logit_sb[:, n % 2, tok, :], ACT.Exp,
                                                           bias=bias, accum_out=den)
                            else:
                                src = psum[:, SCORES + banks[0], tok * SEQ:tok * SEQ + SEQ]
                                ins = nc.scalar.activation(probs[:, n % 3, tok, :], src, ACT.Exp, bias=bias, scale=SCALE,
                                                           accum_out=den)
                        if kind == "c":
                            ins = nc.scalar.activation(sinkexp[:, s, :], negmax[:, s, :], ACT.Exp, bias=sink_sb[:, h:h + 1])
                        ins.then_inc(exp_done, 1)
                        if kind == "a" and h + 2 < 8:
                            act.dma_start(bias_sb[:, h % 2], a_bias[h + 2]).then_inc(bias_loaded[h % 2], 16)

            act.dma_start(gain_x[:, 0:2, :], attn_gain).then_inc(const_loaded, 16)
            act.wait_ge(const_loaded, CONST)
            nc.scalar.activation(table_warm[:], gain_x[:, 0, 0:1], ACT.Exp, scale=0.0)

            def input_hi(j):
                for half in range(2):
                    fill_to_xt(2 * j + half + 1, half, 4 * j + 2 * half, 0, 4 * j + 2 * half)

            def input_ssq(j):
                act.wait_ge(x_loaded[j], 16)
                if j:
                    act.wait_ge(ssq_done, j)
                for tok in range(TOK):
                    ins = nc.scalar.activation(stage[2][:, tok, :], x_res[:, tok, j * N:(j + 1) * N], ACT.Square,
                                               accum_out=ssq[:, tok, j:j + 1])
                ins.then_inc(ssq_done, 1)

            for layer in range(2):
                m, pi, po, pu, pd = mixers[layer], *(ph[s, layer] for s in ("in", "out", "up", "down"))

                def out_tile(n, first):
                    for k in range(KU):
                        if k == LEAD and first:
                            evacuate(layer, len(m.tiles) - 1)
                        split(n * KU + (po["u"] + k), k % RING)
                        if first:
                            attention(layer, KU * len(m.tiles) + k - LEAD)
                        elif k == LEAD + 1:
                            residual_hi(layer, "out", n - 1)
                        elif k == LEAD + 2:
                            residual_ssq(layer, "out", n - 1)

                for p in range(len(m.tiles)):
                    for k in range(KU):
                        u = pi["u"] + KU * p + k
                        if k == LEAD and p:
                            evacuate(layer, p - 1)
                        if layer == 0 and p == 0 and k % 2 == 0:
                            input_hi(k // 2)
                        split(u, k % RING, ring_full=u >= RING)
                        if layer == 0 and p == 0 and k % 2 == 1:
                            input_ssq(k // 2)
                        attention(layer, KU * p + k - LEAD)
                        if layer == 1 and p == 0 and k == LEAD + 1:
                            residual_hi(0, "down", XT - 1)
                        if layer == 1 and p == 0 and k == LEAD + 2:
                            residual_ssq(0, "down", XT - 1)
                            act.wait_ge(unit_used, pi["u"])
                            act.dma_start(partial_sb[:], partial).then_inc(cd_const_loaded, 16)
                            act.dma_start(cd_gain_sb[:], cd_gain).then_inc(cd_const_loaded, 16)
                out_tile(0, True)
                for t in range(m.ticks - LEAD, m.ticks + 2):
                    attention(layer, t)
                with act.Fori(0, XT - 1) as j:
                    out_tile(j + 1, False)

                def up_tile(i, first):
                    for half in range(2):
                        for k in range(KU):
                            if half == 1 and k == LEAD:
                                if first:
                                    act.wait_ge(rstd_ready, 2 * layer + 2)
                                    act.wait_ge(x_stored, RES["down", layer] + 1)
                                silu(layer, i)
                            split(i * (2 * KU) + (pu["u"] + half * KU + k), k % RING)
                            if first and half == 0 and k == LEAD + 1:
                                residual_hi(layer, "out", XT - 1)
                            if first and half == 0 and k == LEAD + 2:
                                residual_ssq(layer, "out", XT - 1)
                            if not first and half == 0 and k == LEAD + 1:
                                hidden_hi(layer, i - 1)

                up_tile(0, True)
                with act.Fori(0, HT - 1) as j:
                    up_tile(j + 1, False)

                def down_tile(n, first):
                    for k, (_, nch) in enumerate(DOWN_UNITS):
                        split(n * DU + (pd["u"] + k), k % RING, nch)
                        if first:
                            if k == LEAD + 1:
                                hidden_hi(layer, HT - 1)
                        elif layer == 0:
                            if k == LEAD + 1:
                                residual_hi(layer, "down", n - 1)
                            if k == LEAD + 2:
                                residual_ssq(layer, "down", n - 1)
                        elif k == LEAD + 1:
                            store(n - 1)

                down_tile(0, True)
                with act.Fori(0, XT - 1) as j:
                    down_tile(j + 1, False)
            store(XT - 1)
            act.wait_ge(stored, 16 * TOK * (XT + 1))

        @block.vector
        def _(dve):
            step = Steps(dve, dve_step)

            def split(u, slot, n=UC):
                dve.wait_ge(hi_ready, u + 1)
                nc.vector.tensor_tensor(w_lo[:, slot, 0:n, :], w_raw[:, slot, 0:n, :],
                                        w_hi[:, slot, 0:n, :].bitcast(F32), ALU.subtract).then_inc(lo_ready, 1)

            def tok_done(pair, tok, uses, units):
                if tok == 0:
                    dve.wait_ge(acc_done[pair], uses)
                else:
                    dve.wait_ge(unit_used, units)

            def fill_to_xt(hi_count, bank, chunk, gain, gain_col):
                dve.wait_ge(t_hi, hi_count)
                for c in range(2):
                    hi = xt_hi[:, bass.ds(chunk + c, 1), :].rearrange("p c t -> p (c t)")
                    lo = xt_lo[:, bass.ds(chunk + c, 1), :].rearrange("p c t -> p (c t)")
                    ins = nc.vector.scalar_tensor_tensor(out=lo, in0=t_bank(bank)[:, c, :],
                                                         scalar=gain_x[:, gain, bass.ds(gain_col + c, 1)],
                                                         in1=hi.bitcast(F32), op0=ALU.mult, op1=ALU.subtract)
                ins.then_inc(t_read[bank], 1)

            def residual_add(layer, name, n):
                if (name, layer) == ("down", 1):
                    dve.wait_ge(x_stored, RES[name, layer] + 1)
                    dve.wait_ge(stored, n * (16 * TOK) + 16 * TOK)
                else:
                    dve.wait_ge(x_stored, n + (RES[name, layer] + 1))
                    dve.wait_ge(ssq_done, n + XT * LN_OF[name, layer])
                uses, units = residual_acc(layer, name, n)
                for tok in range(TOK):
                    tok_done(0, tok, uses, units)
                    ins = nc.vector.tensor_tensor(stage[0][:, tok, :], ACC[0][:, tok, :],
                                                  x_res[:, tok, bass.ds(n * N, N)], ALU.add)
                    ins.then_inc(acc_free[0], 1)

            def residual_lo(layer, name, n):
                gain = GAIN_OF[LN_OF[name, layer]]
                for half in range(2):
                    fill_to_xt(n * 2 + (ph[name, layer]["th"] + half + 1), half, n * 4 + 2 * half, gain,
                               n * 4 + 2 * half)

            def mean_square(ln):
                dve.wait_ge(ssq_done, XT * (ln + 1))
                nc.vector.tensor_reduce(msq[:], ssq[:], AX.X, ALU.add).then_inc(msq_ready, 1)

            def hidden(layer, i):
                pu = ph["up", layer]
                dve.wait_ge(acc_free[0], i * 2 + (2 * pu["a"] + 2))
                for tok in range(TOK):
                    tok_done(1, tok, i + (pu["b"] + 1), (i + 1) * (2 * KU) + pu["u"])
                    ins = nc.vector.scalar_tensor_tensor(out=stage[1][:, tok, :], in0=ACC[1][:, tok, :],
                                                         scalar=rstd[:, 2 * layer + 1, tok:tok + 1],
                                                         in1=stage[0][:, tok, :], op0=ALU.mult, op1=ALU.mult)
                    ins.then_inc(acc_free[1], 1)

            def hidden_lo(layer, i):
                for half in range(2):
                    dve.wait_ge(t_hi, i * 2 + (ph["up", layer]["th"] + half + 1))
                    cs = bass.ds(i * 4 + 2 * half, 2)
                    ins = nc.vector.tensor_tensor(ht_lo[:, cs, :], t_bank(half), ht_hi[:, cs, :].bitcast(F32),
                                                  ALU.subtract)
                    ins.then_inc(t_read[half], 1)

            def rotate_axial(which):
                nh = 4 if which == 0 else 2
                n2, n1, n0 = (heads_of(stage[k], nh) for k in (2, 1, 0))
                cos = axial_sb[:, 2 * which].unsqueeze(2).broadcast_to([P, TOK, nh, DH])
                nc.vector.tensor_tensor(n1, n2, cos, ALU.mult)
                for tok in range(TOK):
                    for s in range(2):
                        pair = "p h (a s j) -> p h a s j"
                        dst = n0[:, tok].rearrange(pair, a=2, s=2)[:, :, :, s, :]
                        src = n2[:, tok].rearrange(pair, a=2, s=2)[:, :, :, 1 - s, :]
                        sin = axial_sb[:, 2 * which + 1, tok].rearrange("p (a s j) -> p a s j", a=2, s=2)[:, :, s, :]
                        ins = nc.vector.tensor_tensor(dst, src, sin.unsqueeze(1).broadcast_to([P, nh, 2, DH // 4]),
                                                      ALU.mult)
                step.then(ins)
                nc.vector.tensor_tensor(n0, n0, n1, ALU.add).then_inc(qk_normed, 1)

            def rotate_partial(which):
                n2, n1, n0 = (heads_of(stage[k], 4) for k in (2, 1, 0))
                cos = partial_sb[:, which, 0].unsqueeze(2).broadcast_to([P, TOK, 4, 32])
                nc.vector.tensor_tensor(n1[:, :, :, 0:32], n2[:, :, :, 0:32], cos, ALU.mult)
                for s in range(2):
                    sin = partial_sb[:, which, 1, :, 16 * s:16 * s + 16].unsqueeze(2).broadcast_to([P, TOK, 4, 16])
                    nc.vector.tensor_tensor(n0[:, :, :, 16 * s:16 * s + 16],
                                            n2[:, :, :, 16 - 16 * s:32 - 16 * s], sin, ALU.mult)
                flat0, flat2 = (stage[k][:].rearrange("p t (h d) -> p (t h) d", d=DH) for k in (0, 2))
                g = cd_gain_sb[:, which, 32:DH].unsqueeze(1).broadcast_to([P, 8, DH - 32])
                step.then(nc.vector.tensor_tensor(flat0[:, :, 32:DH], flat2[:, :, 32:DH], g, ALU.mult))
                nc.vector.tensor_tensor(n0[:, :, :, 0:32], n0[:, :, :, 0:32], n1[:, :, :, 0:32],
                                        ALU.add).then_inc(qk_normed, 1)

            def attention(layer, t):
                m = mixers[layer]
                for n in m.pv:
                    kind, h, _, _, at = m.items[n]
                    if t == at + 1:
                        r = m.pv_rank[n]
                        dve.wait_ge(ot_hi_ready, m.head0 + r + 1)
                        c = CHUNK_OF[kind] + h
                        nc.vector.tensor_tensor(ht_lo[:, c, :], o_bank(kind, h), ht_hi[:, c, :].bitcast(F32),
                                                ALU.subtract).then_inc(ot_ready, 1)
                for q, p in enumerate(m.qk_tiles):
                    _, kind, h0 = m.tiles[p]
                    nh = 2 if kind == "kv_b" else 4
                    if t == m.qk_tick(p, 1):
                        dve.wait_ge(sq_ready, m.qk0 + q + 1)
                        nc.vector.tensor_reduce(head_ssq[:, :, 0:nh], heads_of(stage[1], nh), AX.X,
                                                ALU.add).then_inc(hssq_ready, 1)
                    if t == m.qk_tick(p, 2):
                        dve.wait_ge(hrstd_ready, m.qk0 + q + 1)
                        r = head_rstd[:, :, 0:nh].unsqueeze(3).broadcast_to([P, TOK, nh, DH])
                        ins = nc.vector.tensor_tensor(heads_of(stage[2], nh), heads_of(stage[0], nh), r, ALU.mult)
                        if kind in ("q_a", "k_a"):
                            ins.then_inc(qk_normed, 1)
                            continue
                        step.then(ins)
                        if kind in ("q_b", "kv_b"):
                            rotate_axial(0 if kind == "q_b" else 1)
                        else:
                            rotate_partial({"q_c": 0, "k_c": 1, "q_d": 2, "k_d": 3}[kind])
                for n, (kind, h, at, *_) in enumerate(m.items):
                    s = n % 4
                    if t == at + 1:
                        dve.wait_ge(l_full, m.head0 + n + 1)
                        if kind == "a":
                            dve.wait_ge(bias_loaded[h % 2], 16 * (h // 2 + 1))
                            b = m.banks[n][0]
                            src = psum[:, SCORES + b, :].rearrange("p (t k) -> p t k", t=TOK)
                            ins = nc.vector.scalar_tensor_tensor(out=logit_sb[:, n % 2], in0=src, scalar=SCALE,
                                                                 in1=bias_sb[:, h % 2], op0=ALU.mult, op1=ALU.add)
                            ins.then_inc(biased, 1)
                            dve.wait_ge(biased, h + 1)
                            step.then(nc.vector.tensor_reduce(rowmax[:, s], logit_sb[:, n % 2], AX.X, ALU.max))
                            nc.vector.tensor_scalar(negmax[:, s], rowmax[:, s], -1.0, None,
                                                    ALU.mult).then_inc(negmax_ready, 1)
                            continue
                        if kind == "d":
                            for tok in range(TOK):
                                ins = nc.vector.tensor_reduce(rowmax[:, s, tok:tok + 1],
                                                              psum[:, SCORES:SCORES + 3, tok * SEQ:tok * SEQ + SEQ],
                                                              AX.XY, ALU.max)
                            step.then(ins)
                        else:
                            b = m.banks[n][0]
                            src = psum[:, SCORES + b, :].rearrange("p (t k) -> p t k", t=TOK)
                            step.then(nc.vector.tensor_reduce(rowmax[:, s], src, AX.X, ALU.max))
                        if kind == "c":
                            ins = nc.vector.tensor_scalar(negmax[:, s], rowmax[:, s], -SCALE, neg_sink[:, h:h + 1],
                                                          ALU.mult, ALU.min)
                        else:
                            ins = nc.vector.tensor_scalar(negmax[:, s], rowmax[:, s], -SCALE, None, ALU.mult)
                        ins.then_inc(negmax_ready, 1)
                    if t == m.exp_tick(n) + 1:
                        dve.wait_ge(exp_done, m.head0 + n + 1)
                        if kind == "c":
                            step.then(nc.vector.tensor_tensor(denom[:, s], denom[:, s], sinkexp[:, s], ALU.add))
                        if kind == "d":
                            step.then(nc.vector.tensor_tensor(probs[:, 0], probs[:, 0], probs[:, 1], ALU.add))
                            step.then(nc.vector.tensor_tensor(probs[:, 0], probs[:, 0], probs[:, 2], ALU.add))
                        step.then(nc.vector.reciprocal(rdenom[:, s], denom[:, s]))
                        slot = 0 if kind == "d" else n % 3
                        for tok in range(TOK):
                            ins = nc.vector.tensor_scalar(probs[:, slot, tok, :], probs[:, slot, tok, :],
                                                          rdenom[:, s, tok:tok + 1], None, ALU.mult)
                        ins.then_inc(probs_ready, 1)

            def input_lo(j):
                for half in range(2):
                    fill_to_xt(2 * j + half + 1, half, 4 * j + 2 * half, 0, 4 * j + 2 * half)

            for layer in range(2):
                m, pi, po, pu, pd = mixers[layer], *(ph[s, layer] for s in ("in", "out", "up", "down"))

                def out_tile(n, first):
                    for k in range(KU):
                        if k == LEAD - 1 and not first:
                            residual_add(layer, "out", n - 1)
                        split(n * KU + (po["u"] + k), k % RING)
                        if first:
                            attention(layer, KU * len(m.tiles) + k - LEAD)
                        elif k == LEAD + 2:
                            residual_lo(layer, "out", n - 1)

                for p in range(len(m.tiles)):
                    for k in range(KU):
                        if layer == 1 and p == 0 and k == LEAD - 1:
                            residual_add(0, "down", XT - 1)
                        if layer == 0 and p == 0 and k % 2 == 0:
                            input_lo(k // 2)
                        split(pi["u"] + KU * p + k, k % RING)
                        if layer == 0 and p == 0 and k == KU - 1:
                            mean_square(0)
                        attention(layer, KU * p + k - LEAD)
                        if layer == 0 and p == 1 and k == 0:
                            dve.wait_ge(const2_loaded, CONST2)
                            step.then(nc.vector.tensor_scalar(neg_sink[:], sink_sb[:], -1.0, None, ALU.mult))
                            g = b_gain_sb[:].unsqueeze(2).broadcast_to([P, 4, TOK, DH])
                            step.then(nc.vector.tensor_tensor(axial_sb[:], axial_sb[:], g, ALU.mult))
                        if layer == 1 and p == 0 and k == LEAD + 2:
                            residual_lo(0, "down", XT - 1)
                        if layer == 1 and p == 0 and k == LEAD + 3:
                            mean_square(2)
                        if layer == 1 and p == 0 and k == LEAD + 4:
                            dve.wait_ge(cd_const_loaded, 32)
                            g = cd_rot_sb[:].rearrange("p w k d -> p (w k) d").unsqueeze(2).broadcast_to([P, 8, TOK, 32])
                            tab = partial_sb[:].rearrange("p w k t d -> p (w k) t d")
                            step.then(nc.vector.tensor_tensor(tab, tab, g, ALU.mult))
                out_tile(0, True)
                for t in range(m.ticks - LEAD, m.ticks + 2):
                    attention(layer, t)
                with dve.Fori(0, XT - 1) as j:
                    out_tile(j + 1, False)

                def up_tile(i, first):
                    for half in range(2):
                        for k in range(KU):
                            if half == 0 and k == LEAD - 1:
                                if first:
                                    residual_add(layer, "out", XT - 1)
                                else:
                                    hidden(layer, i - 1)
                            split(i * (2 * KU) + (pu["u"] + half * KU + k), k % RING)
                            if half == 0 and k == LEAD + 2:
                                if first:
                                    residual_lo(layer, "out", XT - 1)
                                else:
                                    hidden_lo(layer, i - 1)
                            if first and half == 0 and k == LEAD + 3:
                                mean_square(2 * layer + 1)

                up_tile(0, True)
                with dve.Fori(0, HT - 1) as j:
                    up_tile(j + 1, False)

                def down_tile(n, first):
                    for k, (_, nch) in enumerate(DOWN_UNITS):
                        if k == LEAD - 1:
                            if first:
                                hidden(layer, HT - 1)
                            else:
                                residual_add(layer, "down", n - 1)
                        split(n * DU + (pd["u"] + k), k % RING, nch)
                        if k == LEAD + 2:
                            if first:
                                hidden_lo(layer, HT - 1)
                            elif layer == 0:
                                residual_lo(layer, "down", n - 1)

                down_tile(0, True)
                with dve.Fori(0, XT - 1) as j:
                    down_tile(j + 1, False)
            residual_add(1, "down", XT - 1)

        @block.gpsimd
        def _(pool):
            step = Steps(pool, pool_step)
            step.then(nc.gpsimd.memset(minus_half[:], -0.5))
            nc.gpsimd.sem_inc(x_stored, 1)
            nc.gpsimd.sem_inc(stored, 16 * TOK)

            def norm_rstd(ln):
                pool.wait_ge(msq_ready, ln + 1)
                step.then(nc.gpsimd.tensor_scalar(msq_eps[:], msq[:], 1.0 / D_MODEL, EPS, ALU.mult, ALU.add))
                nc.gpsimd.tensor_tensor(rstd[:, ln], msq_eps[:], minus_half[:, 0:TOK], ALU.pow).then_inc(rstd_ready, 1)

            def head_rstds(layer):
                m = mixers[layer]
                for q in range(len(m.qk_tiles)):
                    nh = 2 if m.tiles[m.qk_tiles[q]][1] == "kv_b" else 4
                    pool.wait_ge(hssq_ready, m.qk0 + q + 1)
                    step.then(nc.gpsimd.tensor_scalar(head_eps[:, :, 0:nh], head_ssq[:, :, 0:nh], 1.0 / DH, EPS,
                                                      ALU.mult, ALU.add))
                    half = minus_half[:, 0:TOK * nh].rearrange("p (t h) -> p t h", t=TOK)
                    nc.gpsimd.tensor_tensor(head_rstd[:, :, 0:nh], head_eps[:, :, 0:nh], half,
                                            ALU.pow).then_inc(hrstd_ready, 1)

            def keep_residual(layer, name):
                with pool.Fori(0, XT) as n:
                    pool.wait_ge(acc_free[0], n * 2 + (2 * ph[name, layer]["a"] + 2))
                    nc.gpsimd.tensor_copy(x_res[:, :, bass.ds(n * N, N)], stage[0][:]).then_inc(x_stored, 1)

            norm_rstd(0)
            head_rstds(0)
            keep_residual(0, "out")
            norm_rstd(1)
            keep_residual(0, "down")
            norm_rstd(2)
            head_rstds(1)
            keep_residual(1, "out")
            norm_rstd(3)


def rope_tables(pos, dims, theta):
    import numpy as np
    half = dims // 2
    inv = np.exp((-np.log(theta) * np.arange(half) * (2.0 / dims))).astype(np.float32)
    ang = (pos.astype(np.float32)[:, None] * inv[None, :]).astype(np.float32).astype(np.float64)
    cos, sin = np.cos(ang), np.sin(ang)
    return (np.concatenate([cos, cos], 1).astype(np.float32), np.concatenate([-sin, sin], 1).astype(np.float32))


def kernel(**inputs):
    import numpy as np
    import concourse.bacc as bacc
    from concourse import mybir as mb
    from concourse.bass_utils import run_bass_kernel_spmd as run

    a = {k: np.asarray(v) for k, v in inputs.items()}
    cols, rows_n, kr, win = 64, SEQ // 64, min(8, SEQ // 64), 16
    pos = np.arange(SEQ)

    def bcast(v):
        return np.ascontiguousarray(np.broadcast_to(v[None], (P,) + v.shape))

    def by_partition(t):
        return np.ascontiguousarray(np.moveaxis(t.reshape(TOK, P, *t.shape[1:]), 0, 1))

    r, c = pos // cols, pos % cols
    start_r = np.clip(r - kr // 2, 0, rows_n - kr)
    start_c = np.clip(c - win // 2, 0, cols - win)
    inside = ((r[None] >= start_r[:, None]) & (r[None] < start_r[:, None] + kr)
              & (c[None] >= start_c[:, None]) & (c[None] < start_c[:, None] + win))
    dr = np.clip(r[None] - r[:, None] + 7, 0, 14)
    dc = np.clip(c[None] - c[:, None] + 15, 0, 30)
    bias = np.full((8, SEQ, SEQ), -2.0 ** 100, a["a_rpb"].dtype)
    bias[:, inside] = a["a_rpb"][0][:, dr[inside], dc[inside]]
    bias = np.ascontiguousarray(bias.reshape(8, TOK, P, SEQ).transpose(0, 2, 1, 3))

    rc, rs = rope_tables(r, 64, 10000.0)
    cc, cs = rope_tables(c, 64, 10000.0)
    cos, sin = np.concatenate([rc, cc], 1), np.concatenate([rs, cs], 1)
    axial = np.ascontiguousarray(np.stack([by_partition(t) for t in (cos, sin, cos, sin)], 1))
    swap = np.arange(DH).reshape(2, 2, 32)[:, ::-1].ravel()
    bq, bk = a["b_q_norm"][0], a["b_k_norm"][0]
    b_gain = bcast(np.stack([bq, bq[swap], bk, bk[swap]]))
    pc, psn = rope_tables(pos, 32, 500000.0)
    pair = np.stack([by_partition(pc), by_partition(psn)], 1)
    partial = np.ascontiguousarray(np.stack([pair] * 4, 1))
    swap32 = np.arange(32).reshape(2, 16)[::-1].ravel()
    norms = [a[k][0] for k in ("c_q_norm", "c_k_norm", "d_q_norm", "d_k_norm")]
    cd_gain = bcast(np.stack(norms))
    cd_rot = bcast(np.stack([np.stack([g[:32], g[swap32]]) for g in norms]))

    diff = pos[None] - pos[:, None]
    valid = [np.abs(diff) <= 128] + [(np.abs(diff) <= w // 2) & (diff % d == 0) for w, d in
                                     ((128, 1), (512, 4), (2048, 16))]
    bf16 = mb.dt.np(mb.dt.bfloat16)
    masks = np.stack([by_partition(np.where(v, 0.0, -2.0 ** 100).astype(np.float32)) for v in valid], 1).astype(bf16)

    arrays = {
        "x": a["x"][0], "attn_gain": np.ascontiguousarray(a["attn_norm"].reshape(2, KC, P).transpose(2, 0, 1)),
        "ffn_gain": np.ascontiguousarray(a["ffn_norm"].reshape(2, KC, P).transpose(2, 0, 1)),
        "ab_w_in": a["ab_w_in"][0], "ab_w_out": a["ab_w_out"][0],
        "a_gain": np.ascontiguousarray(np.stack([a["a_q_norm"][0], a["a_k_norm"][0]], 1)),
        "a_bias": bias, "b_gain": b_gain, "cd_w_in": a["cd_w_in"][0], "cd_w_out": a["cd_w_out"][0],
        "cd_gain": cd_gain, "cd_gain_rot": cd_rot, "sink": bcast(a["c_sink"][0]),
        "w_gate": a["w_gate"], "w_up": a["w_up"], "w_down": a["w_down"],
        "ident": np.eye(P, dtype=np.float32), "ident16": np.eye(P, dtype=np.float32).astype(bf16),
        "masks": masks, "axial": axial, "partial": partial,
    }
    nc = bacc.Bacc("TRN2", target_bir_lowering=False, num_devices=1, dynamic_dma_scratch_size=2048)
    feeds, args = {}, []
    for name, v in arrays.items():
        feeds[f"in_{name}"] = np.ascontiguousarray(v)
        args.append(nc.dram_tensor(f"in_{name}", v.shape, mb.dt.from_np(v.dtype), kind="ExternalInput").ap())
    out = nc.dram_tensor("out", (SEQ, D_MODEL), mb.dt.float32, kind="ExternalOutput").ap()
    encoder(nc, *args, out)
    res = run(nc, [feeds], core_ids=[0])
    return res.results[0]["out"].reshape(1, SEQ, D_MODEL)
```
